# Optimizing a Trainium2 kernel written in Bass

```python
import math
import jax, jax.numpy as jnp
from jax import lax
import numpy as np

D_MODEL = 1024
BATCH = 1
SEQ = 512
DEPTH = 2
DEC_BATCH = 8
DEC_SEQ = 1
PAST_LEN = 512
PAGE_SIZE = 128

N_SB_LAYERS = (DEPTH + 1) // 2
N_RET_LAYERS = DEPTH // 2
SB_HEADS = 8
SB_HEAD_DIM = 64
SB_WIDTH = SB_HEADS * SB_HEAD_DIM
QBLOCK = 128
SB_BIAS_INIT = -6.0
POOL_WINDOWS = (2, 4, 8, 16)
POOL_GROUP = 128
POOL_WIDTH = len(POOL_WINDOWS) * POOL_GROUP
POOL_BUF = max(POOL_WINDOWS) - 1
EVEN_IN = 3 * SB_WIDTH + POOL_WIDTH
EVEN_MIX = SB_WIDTH + POOL_WIDTH
RET_HEADS = 4
RET_QK_DIM = 256
RET_V_DIM = 512
RET_QK_WIDTH = RET_HEADS * RET_QK_DIM
RET_V_WIDTH = RET_HEADS * RET_V_DIM
ODD_IN = 2 * RET_QK_WIDTH + 2 * RET_V_WIDTH
RET_CHUNK = 128
ROPE_BASE = 10000.0
D_FF = 2816
N_SUB = 3
NORM_EPS = 1e-6

kernel_name = 'hybrid_stickbreak_pool_retention_step'

def rmsnorm(x, g):
    xf = x.astype(jnp.float32)
    y = xf * lax.rsqrt(jnp.mean(xf * xf, axis=-1, keepdims=True) + NORM_EPS)
    return (y * g.astype(jnp.float32)).astype(x.dtype)

def adaln_pre(x, m, g):
    return rmsnorm(x, g) * (1 + m[:, 1][:, None]) + m[:, 0][:, None]

def adaln_post(x, y, m, g, res_w):
    return x + res_w * m[:, 2][:, None] * rmsnorm(y, g)

def swiglu(h, w_in, w_out):
    gt, up = jnp.split(h @ w_in, 2, axis=-1)
    return (jax.nn.silu(gt) * up) @ w_out

def rotary(x, pos):
    half = x.shape[-1] // 2
    inv = ROPE_BASE ** (-jnp.arange(half, dtype=jnp.float32) / half)
    ang = pos[:, None] * inv[None, :]
    cos = jnp.cos(ang)[None, :, None, :]
    sin = jnp.sin(ang)[None, :, None, :]
    xf = x.astype(jnp.float32)
    x1, x2 = xf[..., :half], xf[..., half:]
    return jnp.concatenate([x1 * cos - x2 * sin, x1 * sin + x2 * cos], axis=-1).astype(x.dtype)

def stick_breaking(q, k, v, q_pos0, sb_bias):
    T = q.shape[1]
    scale = SB_HEAD_DIM ** -0.5
    bias = sb_bias.astype(jnp.float32)[None, :, None, None]
    outs = []
    for qs in range(0, T, QBLOCK):
        qe = min(qs + QBLOCK, T)
        kend = max(q_pos0 + qe - 1, 1)
        qb, kb, vb = q[:, qs:qe], k[:, :kend], v[:, :kend]
        q_pos = q_pos0 + jnp.arange(qs, qe)
        k_pos = jnp.arange(kend)
        mask = k_pos[None, :] < q_pos[:, None]
        z = jnp.einsum('bqhd,bkhd->bhqk', qb, kb).astype(jnp.float32) * scale + bias
        log_1m = jnp.where(mask, jax.nn.log_sigmoid(-z), 0.0)
        log_w = jax.nn.log_sigmoid(z) + lax.cumsum(log_1m, axis=3, reverse=True) - log_1m
        w = jnp.where(mask, jnp.exp(log_w), 0.0)
        outs.append(jnp.einsum('bhqk,bkhd->bqhd', w.astype(vb.dtype), vb))
    return jnp.concatenate(outs, axis=1)

def multiscale_pool(u_ext, n_new, pool_w, pool_scale):
    B, PT, C = u_ext.shape
    n_prev = PT - n_new
    cs = jnp.concatenate([jnp.zeros((B, 1, C), jnp.float32),
                          jnp.cumsum(u_ext.astype(jnp.float32), axis=1)], axis=1)
    end = n_prev + 1 + jnp.arange(n_new)
    cs_end = cs[:, end]
    means = []
    for gi, w in enumerate(POOL_WINDOWS):
        start = jnp.maximum(end - w, 0)
        cnt = (end - start).astype(jnp.float32)[None, :, None]
        lo, hi = gi * POOL_GROUP, (gi + 1) * POOL_GROUP
        means.append((cs_end[..., lo:hi] - cs[:, start, lo:hi]) / cnt)
    mean = jnp.concatenate(means, axis=-1)
    d = (mean - u_ext[:, n_prev:].astype(jnp.float32)).astype(u_ext.dtype)
    d = d.reshape(B, n_new, len(POOL_WINDOWS), POOL_GROUP)
    y = jnp.einsum('btgc,gcd->btgd', d, pool_w).reshape(B, n_new, POOL_WIDTH)
    return y * pool_scale

def even_mixer(h, w_in, sb_bias, pool_w, pool_scale, w_out, k_past, v_past, pool_buf):
    B, T, _ = h.shape
    q, k, v, u = jnp.split(h @ w_in, [SB_WIDTH, 2 * SB_WIDTH, 3 * SB_WIDTH], axis=-1)
    q = q.reshape(B, T, SB_HEADS, SB_HEAD_DIM)
    k = k.reshape(B, T, SB_HEADS, SB_HEAD_DIM)
    v = v.reshape(B, T, SB_HEADS, SB_HEAD_DIM)
    if k_past is None:
        k_all, v_all, u_ext, pos0 = k, v, u, 0
    else:
        k_all = jnp.concatenate([k_past.astype(k.dtype), k], axis=1)
        v_all = jnp.concatenate([v_past.astype(v.dtype), v], axis=1)
        u_ext = jnp.concatenate([pool_buf.astype(u.dtype), u], axis=1)
        pos0 = k_past.shape[1]
    o_sb = stick_breaking(q, k_all, v_all, pos0, sb_bias).reshape(B, T, SB_WIDTH)
    o_pool = multiscale_pool(u_ext, T, pool_w, pool_scale)
    y = jnp.concatenate([o_sb, o_pool], axis=-1) @ w_out
    return y, k, v, u_ext[:, -POOL_BUF:]

def retention_chunk(S, q, k, v, log_gamma):
    L = q.shape[1]
    i = jnp.arange(L, dtype=jnp.float32)
    diff = i[:, None] - i[None, :]
    decay = jnp.where(diff[None] >= 0,
                      jnp.exp(jnp.maximum(diff, 0.0)[None] * log_gamma[:, None, None]), 0.0)
    scores = jnp.einsum('blhd,bmhd->bhlm', q, k) * decay[None]
    intra = jnp.einsum('bhlm,bmhe->blhe', scores, v)
    cross = jnp.einsum('blhd,bhde->blhe', q, S) * jnp.exp((i[:, None] + 1.0) * log_gamma[None, :])[None, :, :, None]
    k_dec = k * jnp.exp((L - 1.0 - i)[:, None] * log_gamma[None, :])[None, :, :, None]
    S_new = jnp.exp(L * log_gamma)[None, :, None, None] * S + jnp.einsum('blhd,blhe->bhde', k_dec, v)
    return S_new, intra + cross

def retention_mixer(h, w_in, w_out, S0, pos0):
    B, T, _ = h.shape
    q, k, v, g = jnp.split(h @ w_in, [RET_QK_WIDTH, 2 * RET_QK_WIDTH, 2 * RET_QK_WIDTH + RET_V_WIDTH], axis=-1)
    pos = pos0 + jnp.arange(T, dtype=jnp.float32)
    q = rotary(q.reshape(B, T, RET_HEADS, RET_QK_DIM), pos).astype(jnp.float32)
    k = rotary(k.reshape(B, T, RET_HEADS, RET_QK_DIM), pos).astype(jnp.float32) * (RET_QK_DIM ** -0.5)
    v = v.reshape(B, T, RET_HEADS, RET_V_DIM).astype(jnp.float32)
    log_gamma = jnp.log(1.0 - jnp.exp2(-5.0 - jnp.arange(RET_HEADS, dtype=jnp.float32)))
    if S0 is None:
        S0 = jnp.zeros((B, RET_HEADS, RET_QK_DIM, RET_V_DIM), jnp.float32)
    else:
        S0 = S0.astype(jnp.float32)
    if T % RET_CHUNK == 0:
        nc = T // RET_CHUNK
        xs = tuple(jnp.moveaxis(a.reshape(B, nc, RET_CHUNK, a.shape[2], a.shape[3]), 1, 0) for a in (q, k, v))
        S, o = lax.scan(lambda s, inp: retention_chunk(s, inp[0], inp[1], inp[2], log_gamma), S0, xs)
        o = jnp.moveaxis(o, 0, 1).reshape(B, T, RET_HEADS, RET_V_DIM)
    else:
        S, o = retention_chunk(S0, q, k, v, log_gamma)
    mu = jnp.mean(o, axis=-1, keepdims=True)
    var = jnp.mean(jnp.square(o - mu), axis=-1, keepdims=True)
    o = ((o - mu) * lax.rsqrt(var + 1e-5)).reshape(B, T, RET_V_WIDTH).astype(h.dtype)
    return (o * jax.nn.silu(g)) @ w_out, S

def run_trunk(x, c, sb_past, pool_past, ret_past, pos0, params):
    (w_ada, b_ada, norm_pre, norm_post, ffn_w_in, ffn_w_out,
     w_in_even, sb_bias, pool_w, pool_scale, w_out_even, w_in_odd, w_out_odd) = params
    B = x.shape[0]
    cond = jax.nn.silu(c)
    new_k, new_v, new_pool, new_ret = [], [], [], []
    for l in range(DEPTH):
        mod = (cond @ w_ada[l] + b_ada[l]).reshape(B, N_SUB, 3, D_MODEL)
        h = adaln_pre(x, mod[:, 0], norm_pre[l, 0])
        x = adaln_post(x, swiglu(h, ffn_w_in[l, 0], ffn_w_out[l, 0]), mod[:, 0], norm_post[l, 0], 0.5)
        h = adaln_pre(x, mod[:, 1], norm_pre[l, 1])
        li = l // 2
        if l % 2 == 0:
            kp = None if sb_past is None else sb_past[li][0]
            vp = None if sb_past is None else sb_past[li][1]
            pb = None if pool_past is None else pool_past[li]
            y, k_new, v_new, buf = even_mixer(h, w_in_even[li], sb_bias[li], pool_w[li], pool_scale[li],
                                              w_out_even[li], kp, vp, pb)
            new_k.append(k_new)
            new_v.append(v_new)
            new_pool.append(buf)
        else:
            s0 = None if ret_past is None else ret_past[li]
            y, S = retention_mixer(h, w_in_odd[li], w_out_odd[li], s0, pos0)
            new_ret.append(S)
        x = adaln_post(x, y, mod[:, 1], norm_post[l, 1], 1.0)
        h = adaln_pre(x, mod[:, 2], norm_pre[l, 2])
        x = adaln_post(x, swiglu(h, ffn_w_in[l, 1], ffn_w_out[l, 1]), mod[:, 2], norm_post[l, 2], 0.5)
    return x, new_k, new_v, new_pool, new_ret

def setup_inputs(seed: int = 0) -> dict:
    key = jax.random.key(seed)
    ks = jax.random.split(key, 22)
    f32 = jnp.float32
    n_pages = PAST_LEN // PAGE_SIZE
    n_used = DEC_BATCH * n_pages
    n_phys = n_used + max(1, n_used // 4)
    nrm = lambda k, shape, s: jax.random.normal(k, shape, f32) * s
    page_table = jax.random.permutation(ks[8], n_phys)[:n_used].reshape(DEC_BATCH, n_pages).astype(jnp.int32)
    return {
        'x_prompt': nrm(ks[0], (BATCH, SEQ, D_MODEL), 1.0),
        'x_sample': nrm(ks[1], (DEC_BATCH, DEC_SEQ, D_MODEL), 1.0),
        'c_prompt': nrm(ks[2], (BATCH, D_MODEL), 1.0),
        'c_sample': nrm(ks[3], (DEC_BATCH, D_MODEL), 1.0),
        'cache_k': nrm(ks[4], (N_SB_LAYERS, n_phys, PAGE_SIZE, SB_HEADS, SB_HEAD_DIM), 1.0),
        'cache_v': nrm(ks[5], (N_SB_LAYERS, n_phys, PAGE_SIZE, SB_HEADS, SB_HEAD_DIM), 1.0),
        'state_pool': nrm(ks[6], (N_SB_LAYERS, DEC_BATCH, POOL_BUF, POOL_WIDTH), 1.0),
        'state_ret': nrm(ks[7], (N_RET_LAYERS, DEC_BATCH, RET_HEADS, RET_QK_DIM, RET_V_DIM), 0.5),
        'page_table': page_table,
        'w_ada': nrm(ks[9], (DEPTH, D_MODEL, N_SUB * 3 * D_MODEL), 0.5 * D_MODEL ** -0.5),
        'b_ada': nrm(ks[10], (DEPTH, N_SUB * 3 * D_MODEL), 0.01),
        'norm_pre': 1.0 + nrm(ks[11], (DEPTH, N_SUB, D_MODEL), 0.05),
        'norm_post': 1.0 + nrm(ks[12], (DEPTH, N_SUB, D_MODEL), 0.05),
        'ffn_w_in': nrm(ks[13], (DEPTH, 2, D_MODEL, 2 * D_FF), D_MODEL ** -0.5),
        'ffn_w_out': nrm(ks[14], (DEPTH, 2, D_FF, D_MODEL), D_FF ** -0.5),
        'w_in_even': nrm(ks[15], (N_SB_LAYERS, D_MODEL, EVEN_IN), D_MODEL ** -0.5),
        'sb_bias': SB_BIAS_INIT + nrm(ks[21], (N_SB_LAYERS, SB_HEADS), 0.1),
        'pool_w': nrm(ks[16], (N_SB_LAYERS, len(POOL_WINDOWS), POOL_GROUP, POOL_GROUP), POOL_GROUP ** -0.5),
        'pool_scale': 1.0 + nrm(ks[17], (N_SB_LAYERS, POOL_WIDTH), 0.1),
        'w_out_even': nrm(ks[18], (N_SB_LAYERS, EVEN_MIX, D_MODEL), EVEN_MIX ** -0.5),
        'w_in_odd': nrm(ks[19], (N_RET_LAYERS, D_MODEL, ODD_IN), D_MODEL ** -0.5),
        'w_out_odd': nrm(ks[20], (N_RET_LAYERS, RET_V_WIDTH, D_MODEL), RET_V_WIDTH ** -0.5),
    }

def reference(x_prompt, x_sample, c_prompt, c_sample, cache_k, cache_v, state_pool, state_ret,
              page_table, w_ada, b_ada, norm_pre, norm_post, ffn_w_in, ffn_w_out,
              w_in_even, sb_bias, pool_w, pool_scale, w_out_even, w_in_odd, w_out_odd):
    params = (w_ada, b_ada, norm_pre, norm_post, ffn_w_in, ffn_w_out,
              w_in_even, sb_bias, pool_w, pool_scale, w_out_even, w_in_odd, w_out_odd)
    db, n_pages = page_table.shape
    past_len = n_pages * cache_k.shape[2]
    y_prompt, kp, vp, pp, rp = run_trunk(x_prompt, c_prompt, None, None, None, 0, params)
    sb_past = []
    for li in range(N_SB_LAYERS):
        kg = cache_k[li][page_table].reshape(db, past_len, SB_HEADS, SB_HEAD_DIM)
        vg = cache_v[li][page_table].reshape(db, past_len, SB_HEADS, SB_HEAD_DIM)
        sb_past.append((kg, vg))
    pool_past = [state_pool[li] for li in range(N_SB_LAYERS)]
    ret_past = [state_ret[li] for li in range(N_RET_LAYERS)]
    y_sample, ks_, vs_, ps_, rs_ = run_trunk(x_sample, c_sample, sb_past, pool_past, ret_past, past_len, params)
    return (y_prompt, y_sample,
            jnp.stack(kp, 0), jnp.stack(vp, 0), jnp.stack(pp, 0), jnp.stack(rp, 0),
            jnp.stack(ks_, 0), jnp.stack(vs_, 0), jnp.stack(ps_, 0), jnp.stack(rs_, 0))


_drawn_inputs = setup_inputs


def setup_inputs(seed=0):
    import zlib

    import numpy as np

    out = dict(_drawn_inputs(seed))
    spreads = {}
    factors = {'sb_bias': 8.0}
    for name, (base, spread) in spreads.items():
        noise = np.random.default_rng([zlib.crc32(name.encode()), seed]).standard_normal(out[name].shape)
        drawn = base * np.exp(spread * noise) if base else spread * noise
        out[name] = __import__('jax').numpy.asarray(drawn.astype(out[name].dtype))
    for name, factor in factors.items():
        out[name] = (out[name] * factor).astype(out[name].dtype)
    return out
```

```python
from contextlib import ExitStack

import concourse.bass as bass
from concourse import mybir

F32 = mybir.dt.float32
F32R = mybir.dt.float32r
I32 = mybir.dt.int32
ACT = mybir.ActivationFunctionType
ALU = mybir.AluOpType
AX = mybir.AxisListType

P = 128
DM = 1024
SEQ = 512
NS = 8
KC = DM // P
HP = SEQ // 2
HS = NS // 2
HT = HP + HS
FF = 2816
FC = FF // P
NB = 1 + NS
HEADS = 8
HD = 64
PAST = 512
PAGES = PAST // P
PHYS = 40
WINDOWS = (2, 4, 8, 16)
BUF = 15
RH = 4
RV = 512
VT = RV // P
EPS = 1e-6

W8 = 8 * P
W11 = 11 * P

PLAN = [("in0", 2 * FC, W8), ("out0", 16, W11), ("evin", 16, W8), ("evout", 8, W8),
        ("in1", 2 * FC, W8), ("out1", 16, W11), ("in2", 2 * FC, W8), ("out2", 16, W11),
        ("odin", 48, W8), ("odout", 16, W8), ("in3", 2 * FC, W8), ("out3", 16, W11)]
BASE, WIDTH = {}, []
for _name, _n, _w in PLAN:
    BASE[_name] = len(WIDTH)
    WIDTH += [_w] * _n
UNITS = len(WIDTH)
SUB = {"out0": 0, "evout": 1, "out1": 2, "out2": 3, "odout": 4, "out3": 5}
CHUNKS = 2 * 9 * KC
INPUTS = ["in0", "evin", "in1", "in2", "odin", "in3"]
AT_NORM = [8, 8, 8, 8, 8, 4, 0]
BEFORE_SUMS = [0, 4, 4, 4, 4, 4, 0]
ADA_IN = {n: 24 * b + 16 + AT_NORM[b] for b, n in enumerate(INPUTS)}
ADA_N = {n: (24 if b < 5 else 8) - AT_NORM[b] for b, n in enumerate(INPUTS)}


def width(u):
    return WIDTH[u] if u < UNITS else 0


def decoder_step(nc, x_t, c_t, k_pages, v_pages, pool_past, ret_past, table, w_ada, b_ada, g_pre, g_post,
                 w_in, w_out, w_even, w_evout, w_odd, w_odout, bias_b, pool_w, pool_s, rope_c, rope_s, decay,
                 gammas, pool_r, y_t, k_t, v_t, pool_p, pool_n, ret_p, ret_n):
    with ExitStack() as ctx:
        def sem(name):
            return ctx.enter_context(nc.semaphore(name))

        top = [nc.sbuf_base + (-nc.sbuf_base) % 64]

        def at(name, shape, offset, dt=F32):
            return nc.alloc_sbuf_tensor_at(name, [P] + shape, dt, offset=offset)

        def size(shape):
            n = 4
            for d in shape:
                n *= d
            return n

        def sb(name, shape, dt=F32):
            t = at(name, shape, top[0], dt)
            top[0] += (size(shape) + 63) // 64 * 64
            return t

        X = sb("X", [KC, 2, HT])
        HH = sb("HH", [KC, 2, HT], F32R)
        low_at = top[0]
        HL = sb("HL", [KC, 2, HT], F32R)
        Y = at("Y", [KC, 2, HT], low_at)
        hi_at = low_at - size([KC, 2, HT])
        G_at = top[0]
        GH = sb("GH", [FC, 2, HT], F32R)
        GL = sb("GL", [FC, 2, HT], F32R)
        G_end = top[0]
        AFIRST = at("AFIRST", [16, W8], G_at)
        RAW = sb("RAW", [2, W11])
        WH = sb("WH", [2, W11], F32R)
        WL = sb("WL", [2, W11], F32R)
        AW = sb("AW", [2, W8])
        MOD = sb("MOD", [CHUNKS, NB])
        CS = sb("CS", [KC, NB])
        SA1 = sb("SA1", [CHUNKS])
        SA2 = sb("SA2", [CHUNKS])
        ONES = sb("ONES", [P])
        ACC = sb("ACC", [2, HT])
        sq_at = top[0]
        SQ = sb("SQ", [2, 2, HT])
        sg_at = top[0]
        SG = sb("SG", [2, 2, HT])
        VAR = sb("VAR", [2, HT])
        RS = sb("RS", [2, HT])
        ns_at = top[0]
        NT = sb("NT", [2, HT])
        IDENT = sb("IDENT", [P])
        SR = sb("SR", [2, RV])
        assert top[0] <= nc.sbuf_usable_end, (top[0], nc.sbuf_usable_end)
        GAIN = at("GAIN", [96], ns_at)
        G32 = SQ

        g = G_at
        VF = at("VF", [4, SEQ], g)
        OH = at("OH", [KC, 2, HT], g, F32R)
        OL = at("OL", [KC, 2, HT], g + size([KC, 2, HT]), F32R)
        g += 2 * size([KC, 2, HT])
        QP = at("QP", [4, SEQ], g); g += size([4, SEQ])
        KP = at("KP", [4, SEQ], g); g += size([4, SEQ])
        VP = at("VP", [4, SEQ], g); g += size([4, SEQ])
        KV = at("KV", [2, PAGES, 4 * P], g); g += size([2, PAGES, 4 * P])
        QKVS = at("QKVS", [12, NS], g); g += size([12, NS])
        QB = at("QB", [4, NS, 2], g); g += size([4, NS, 2])
        BIAS = at("BIAS", [PAGES * NS * HEADS], g); g += size([256])
        TRI = at("TRI", [P], g); g += size([P])
        UP = at("UP", [4, 16 + SEQ], g); g += size([4, 16 + SEQ])
        US = at("US", [4, NS, 16], g); g += size([4, NS, 16])
        PWT = at("PWT", [4, P], g); g += size([4, P])
        RCP = at("RCP", [4, 16], g); g += size([4, 16])
        UD = at("UD", [4, NS], g); g += size([4, NS])
        OS = at("OS", [4, NS], g); g += size([4, NS])
        PSC = at("PSC", [4], g); g += 64
        PT = at("PT", [NS * PAGES], g, I32); g += size([32])
        assert g <= G_end, (g, G_end)
        LEN = [SEQ - P * j for j in range(4)]
        OFF = [sum(LEN[:j]) for j in range(4)]
        CAUSAL = sum(LEN)
        a = hi_at
        ZS = at("ZS", [2, CAUSAL], a); a += size([2, CAUSAL])
        SP = at("SP", [2, CAUSAL], a); a += size([2, CAUSAL])
        ZN = at("ZN", [3, 256], a); a += size([3, 256])
        OF = at("OF", [2, 2, HT], a); a += size([2, 2, HT])
        assert a <= G_at
        UA = at("UA", [4, 16 + SEQ], hi_at)
        UB = at("UB", [4, 16 + SEQ], hi_at + size([4, 16 + SEQ]))

        g = G_at
        O32 = at("O32", [16, 2, HT], g)
        OGL = at("OGL", [16, 2, HT], g, F32R)
        g += size([16, 2, HT])
        OGH = at("OGH", [16, 2, HT], g, F32R)
        QR = at("QR", [2, SEQ], g); g += size([2, SEQ])
        KR = at("KR", [2, SEQ], g); g += size([2, SEQ])
        QRS = at("QRS", [2, NS], g); g += size([2, NS])
        KRS = at("KRS", [2, NS], g); g += size([2, NS])
        PRD = at("PRD", [2, NS], g); g += size([2, NS])
        QKS = at("QKS", [3, NS], g); g += 128
        VSF = at("VSF", [4, NS], g); g += size([4, NS])
        VQ = at("VQ", [4, NS], g); g += size([4, NS])
        XS = at("XS", [2, 4, NS], g); g += size([2, 4, NS])
        KDEC = at("KDEC", [RH, 4], g); g += 64
        VR = at("VR", [4, RV], g); g += size([4, RV])
        KT = at("KT", [4, 2 * P], g); g += size([4, 2 * P])
        SGO = at("SGO", [4, 2, HT], g); g += size([4, 2, HT])
        OO = at("OO", [4, 2, HT], g)
        VFO = at("VFO", [4, 2, HT], g); g += size([4, 2, HT])
        SC = at("SC", [CAUSAL], g)
        RP = at("RP", [2, RV], g); g += size([CAUSAL])
        DEC = at("DEC", [SEQ], g); g += size([SEQ])
        COS = at("COS", [2, HT], g); g += size([2, HT])
        SIN = at("SIN", [2, HT], g); g += size([2, HT])
        TR = at("TR", [3, 2, HT], g); g += size([3, 2, HT])
        assert g <= G_end, (g, G_end)
        SEL = at("SEL", [NS, P], sq_at)
        VS = at("VS", [RV], ns_at)
        SR2 = at("SR2", [2, RV], sg_at)
        STATE = [SR[:, 0, :], SR[:, 1, :], SR2[:, 0, :], SR2[:, 1, :]]

        PS = [ctx.enter_context(nc.psum_tensor(f"PS{i}", [P, 2, 512], F32)) for i in range(4)]
        ST = PS[2]
        ADAP = PS[3]

        x_in = sem("x_in"); c_in = sem("c_in"); tab_in = sem("tab_in")
        raw_in = [sem("raw_in0"), sem("raw_in1")]
        ada_in = [sem("ada_in0"), sem("ada_in1")]
        first_in = [sem(f"first_in{q}") for q in range(4)]
        const_ok = sem("const_ok")
        silu_c = sem("silu_c")
        sa_ok = sem("sa_ok")
        hi_done = sem("hi_done"); lo_done = sem("lo_done"); unit_done = sem("unit_done")
        ada_mm = sem("ada_mm"); ada_evac = sem("ada_evac")
        gate_evac = sem("gate_evac"); up_evac = sem("up_evac"); gh_done = sem("gh_done"); gl_done = sem("gl_done")
        y_act = sem("y_act"); y_dve = sem("y_dve"); acc_step = sem("acc_step")
        sum_done = sem("sum_done"); var_ok = sem("var_ok"); ln_ok = sem("ln_ok"); exp_ok = sem("exp_ok")
        newton = sem("newton"); y_scaled = sem("y_scaled"); x_upd = sem("x_upd")
        sq_ready = sem("sq_ready"); sq_used = sem("sq_used")
        t_ready = sem("t_ready"); samp = sem("samp"); h32_ready = sem("h32_ready"); hh_ready = sem("hh_ready")
        h_ready = sem("h_ready")
        out_done = sem("out_done")

        y_out = sem("y_out")
        ident_z = sem("ident_z")

        ev_act = sem("ev_act"); ev_dve = sem("ev_dve"); ev_in = sem("ev_in"); ev_zero = sem("ev_zero")
        qb_ready = sem("qb_ready")
        kv_in = [sem("kv_in0"), sem("kv_in1")]; kv_used = sem("kv_used")
        vt_done = sem("vt_done"); vp_ready = sem("vp_ready")
        pool_step = sem("pool_step"); d_ready = sem("d_ready"); pool_mm = sem("pool_mm"); pool_evac = sem("pool_evac")
        zn_done = sem("zn_done"); zn_dve = sem("zn_dve"); zn_act = sem("zn_act"); zn_sum = sem("zn_sum")
        z_done = sem("z_done"); z_act = sem("z_act"); z_dve = sem("z_dve")
        e_done = sem("e_done"); l_done = sem("l_done"); sp_done = sem("sp_done"); sp_ok = sem("sp_ok")
        s_done = sem("s_done"); lw_done = sem("lw_done"); w_done = sem("w_done"); w_ok = sem("w_ok")
        o_done = sem("o_done"); o_evac = sem("o_evac"); pv_done = sem("pv_done"); os_ready = sem("os_ready")
        oh_ready = sem("oh_ready"); ol_ready = sem("ol_ready")
        ident_ok = sem("ident_ok")
        EV = BASE["evin"]

        def even_sp(sp, load_unit, load_norm_chunks):
            load_unit("evin", 0, 0)
            load_unit("evin", 0, 1)
            load_norm_chunks(1)
            sp.wait_ge(h_ready, KC + 1)
            for dst, src in ((PWT[:], pool_w), (RCP[:], pool_r), (PSC[:], pool_s), (BIAS[:], bias_b),
                             (US[:, :, :, 0:BUF], pool_past), (PT[0:1, :], table)):
                sp.dma_start(dst, src).then_inc(ev_in, 16)
            for i in range(2, 16):
                load_unit("evin", i - i % 2, i % 2)
            for i in range(8):
                load_unit("evout", i - i % 2, i % 2)

        def even_pe(pe, products, chunk):
            def scores_past(b):
                pe.wait_ge(qb_ready, 1)
                pe.wait_ge(kv_in[b % 2], 64 * (b // 2 + 1))
                for p in range(PAGES):
                    for t in range(4):
                        c = p * 64 + b * HEADS + 2 * t
                        last = nc.tensor.matmul(PS[2][:, 0, c:c + 2], KV[:, b % 2, p, t * P:(t + 1) * P],
                                                QB[:, t, b, :], start=True, stop=True)
                last.then_inc(kv_used, 1)

            def values_past(b):
                n = NS + b
                pe.wait_ge(kv_in[n % 2], 64 * (n // 2 + 1))
                for t in range(4):
                    for p in range(PAGES):
                        c = p * 64 + b * HEADS + 2 * t
                        last = nc.tensor.matmul(PS[3][:, 1, 64 + b * 8 + 2 * t:66 + b * 8 + 2 * t],
                                                KV[:, n % 2, p, t * P:(t + 1) * P], ZN[:, 2, c:c + 2],
                                                start=(p == 0), stop=(p == PAGES - 1))
                last.then_inc(kv_used, 1)

            for i in range(16):
                pe.wait_ge(lo_done, EV + i + 3)
                if i >= 2:
                    pe.wait_ge(ev_dve, i - 1)
                products(i % 2, i % 2, HH, HL, 0, KC, True, True, (h_ready, KC) if i == 0 else None)
                if i < ADA_N["evin"]:
                    chunk(ADA_IN["evin"] + i - i % 2, i % 2)
                if 6 <= i < 14:
                    scores_past(i - 6)
            pe.wait_ge(ident_ok, 3)
            pe.wait_ge(ev_act, 16)
            pe.wait_ge(ev_dve, 16)
            for i in range(4):
                for t in range(4):
                    last = nc.tensor.transpose(PS[i // 2][:, i % 2, t * P:(t + 1) * P],
                                               VF[:, t, i * P:(i + 1) * P], IDENT[:])
                last.then_inc(vt_done, 1)
            pe.wait_ge(zn_dve, 2)
            nc.tensor.matmul(PS[3][:, 0, 64:320], TRI[:], ZN[:, 1, :], start=True, stop=False)
            for p in range(1, PAGES):
                for q in range(p):
                    last = nc.tensor.matmul(PS[3][:, 0, 64 + 64 * q:128 + 64 * q], ONES[:],
                                            ZN[:, 1, 64 * p:64 * p + 64], start=False,
                                            stop=(p == PAGES - 1 and q == p - 1))
            last.then_inc(zn_sum, 1)
            pe.wait_ge(d_ready, 1)
            for g in range(4):
                nc.tensor.matmul(PS[2][:, 1, NS * g:NS * g + NS], PWT[:, g, :], UD[:, g, :],
                                 start=True, stop=True)
            for g in range(4):
                pe.wait_ge(vp_ready, g + 1)
                src = (UA, UB)[g % 2]
                nc.tensor.matmul(PS[g // 2][:, g % 2, 0:SEQ], PWT[:, g, :], src[:, g, 16:16 + SEQ],
                                 start=True, stop=True).then_inc(pool_mm, 1)

            def scores(h):
                t, r = h // 2, HD * (h % 2)
                for j in range(4):
                    n = 4 * h + j
                    if n >= 2:
                        pe.wait_ge(z_dve, n - 1)
                    nc.tensor.matmul(PS[0][:, j % 2, 0:LEN[j]], KP[r:r + HD, t, j * P:(j + 1) * P],
                                     QP[r:r + HD, t, j * P:SEQ], start=True, stop=True).then_inc(z_done, 1)

            pe.wait_ge(pool_evac, 4)
            scores(0)
            for h in range(HEADS):
                if h + 1 < HEADS:
                    scores(h + 1)
                pe.wait_ge(sp_ok, h + 1)
                for i in range(4):
                    n = 4 * h + i
                    if n >= 2:
                        pe.wait_ge(lw_done, n - 1)
                    out = PS[1][:, i % 2, 0:LEN[i]]
                    last = nc.tensor.matmul(out, TRI[:], SP[:, h % 2, OFF[i]:OFF[i] + LEN[i]],
                                            start=True, stop=(i == 3))
                    for j in range(i + 1, 4):
                        last = nc.tensor.matmul(PS[1][:, i % 2, (j - i) * P:LEN[i]], ONES[:],
                                                SP[:, h % 2, OFF[j]:OFF[j] + LEN[j]],
                                                start=False, stop=(j == 3))
                    last.then_inc(s_done, 1)
                pe.wait_ge(w_ok, h + 1)
                if h >= 2:
                    pe.wait_ge(o_evac, h - 1)
                for i in range(4):
                    last = nc.tensor.matmul(PS[2][:, h % 2, i * P:SEQ], VP[:, i, (h // 2) * P:(h // 2 + 1) * P],
                                            SP[:, h % 2, OFF[i]:OFF[i] + LEN[i]],
                                            start=(i == 0), stop=(i == 3))
                last.then_inc(o_done, 1)
                if h == 0:
                    pe.wait_ge(zn_act, 4)
                values_past(h)
            u0 = BASE["evout"]
            pe.wait_ge(ol_ready, 9)
            for n in range(8):
                pe.wait_ge(lo_done, u0 + n + 3)
                pe.wait_ge(y_act, KC + n + 1)
                pe.wait_ge(y_dve, KC + n + 1)
                products(n % 2, n % 2, OH, OL, 0, KC, True, True)

        def halves(ap):
            return ap.rearrange("p (a b) -> p a b", a=2)

        def even_act(act, split_hi, evac_y, load_chunk):
            for i in range(16):
                u = EV + i + 2
                split_hi(u - u % 2, u % 2, width(u))
                act.wait_ge(unit_done, EV + i + 1)
                if i < ADA_N["evin"] - 1:
                    load_chunk(ADA_IN["evin"] + i + 1 - (i + 1) % 2, (i + 1) % 2)
                dst = ((QP, KP, VF)[i // 4][:, i % 4, :] if i < 12 else UP[:, i % 4, 16:16 + SEQ])
                nc.scalar.activation(halves(dst), PS[i % 2][:, :, 0:HP], ACT.Copy).then_inc(ev_act, 1)
            act.wait_ge(zn_dve, 1)
            nc.scalar.activation(ZN[:, 1, :], ZN[:, 0, :], ACT.Abs).then_inc(zn_act, 1)
            act.wait_ge(zn_act, 1)
            nc.scalar.activation(ZN[:, 1, :], ZN[:, 1, :], ACT.Exp, scale=-1.0).then_inc(zn_act, 1)
            act.wait_ge(zn_act, 2)
            nc.scalar.activation(ZN[:, 1, :], ZN[:, 1, :], ACT.Ln, bias=ONES[:, 0:1]).then_inc(zn_act, 1)

            def split_of(m, dst, cols):
                nc.scalar.activation(OH[:, dst, :, 0:cols], OF[:, m % 2, :, 0:cols], ACT.Copy).then_inc(oh_ready, 1)

            for g in range(4):
                act.wait_ge(pool_mm, g + 1)
                if g >= 2:
                    act.wait_ge(ol_ready, g - 1)
                nc.scalar.activation(OF[:, g % 2, :, 0:HP], halves(PS[g // 2][:, g % 2, 0:SEQ]), ACT.Copy,
                                     scale=PSC[:, g:g + 1])
                nc.scalar.activation(OF[:, g % 2, :, HP:HT], halves(PS[2][:, 1, NS * g:NS * g + NS]), ACT.Copy,
                                     scale=PSC[:, g:g + 1]).then_inc(pool_evac, 1)
                act.wait_ge(pool_evac, g + 1)
                split_of(g, 4 + g, HT)
            act.wait_ge(zn_dve, 3)
            nc.scalar.activation(ZN[:, 2, :], ZN[:, 0, :], ACT.Exp).then_inc(zn_act, 1)

            def softplus(h):
                act.wait_ge(z_dve, 4 * h + 4)
                if h >= 2:
                    act.wait_ge(o_done, h - 1)
                nc.scalar.activation(SP[:, h % 2, :], ZS[:, h % 2, :], ACT.Abs).then_inc(z_act, 1)
                act.wait_ge(z_act, h + 1)
                nc.scalar.activation(SP[:, h % 2, :], SP[:, h % 2, :], ACT.Exp, scale=-1.0).then_inc(e_done, 1)
                act.wait_ge(e_done, h + 1)
                nc.scalar.activation(SP[:, h % 2, :], SP[:, h % 2, :], ACT.Ln, bias=ONES[:, 0:1]).then_inc(l_done, 1)

            act.wait_ge(ol_ready, 1)
            softplus(0)
            for h in range(HEADS):
                if h + 1 < HEADS:
                    softplus(h + 1)
                act.wait_ge(lw_done, 4 * h + 4)
                nc.scalar.activation(SP[:, h % 2, :], ZS[:, h % 2, :], ACT.Exp).then_inc(w_done, 1)
                r, t = HD * (h % 2), h // 2
                act.wait_ge(o_done, h + 1)
                if h % 2 == 0:
                    act.wait_ge(ol_ready, 3 + t)
                nc.scalar.activation(OF[r:r + HD, t % 2, :, 0:HP], halves(PS[2][r:r + HD, h % 2, 0:SEQ]),
                                     ACT.Copy).then_inc(o_evac, 1)
                if h % 2:
                    act.wait_ge(o_evac, h + 1)
                    split_of(t, t, HP)
            act.wait_ge(os_ready, 1)
            nc.scalar.activation(OH[:, 0:4, :, HP:HT], OS[:].rearrange("p t (a b) -> p t a b", a=2),
                                 ACT.Copy).then_inc(oh_ready, 1)
            u0 = BASE["evout"]
            for n in range(8):
                u = u0 + n + 2
                split_hi(u - u % 2, u % 2, width(u))
                evac_y(n, n % 2, 1, u0 + n)
            act.wait_ge(out_done, 96)

        def even_dve(dve, split_lo, evac_chunk, clear_acc, add_y):
            nc.vector.memset(UP[:, :, 0:16], 0.0)
            nc.vector.memset(QB[:], 0.0).then_inc(ev_zero, 1)
            for i in range(16):
                u = EV + i + 2
                split_lo(u - u % 2, u % 2, width(u))
                dve.wait_ge(ev_act, i + 1)
                if i == 12:
                    dve.wait_ge(ev_in, 96)
                dst = halves(QKVS[:, i, :] if i < 12 else US[:, i % 4, :, BUF])
                nc.vector.tensor_copy(dst, PS[i % 2][:, :, HP:HT]).then_inc(ev_dve, 1)
                if i == 3:
                    dve.wait_ge(ev_dve, 4)
                    dve.wait_ge(ev_zero, 1)
                    nc.vector.tensor_copy(QB[0:HD, :, :, 0], QKVS[0:HD, 0:4, :])
                    nc.vector.tensor_copy(QB[HD:P, :, :, 1], QKVS[HD:P, 0:4, :]).then_inc(qb_ready, 1)
                if i < ADA_N["evin"]:
                    evac_chunk(ADA_IN["evin"] + i - i % 2, i % 2)
            dve.wait_ge(kv_used, NS)
            nc.vector.scalar_tensor_tensor(ZN[:, 0, :], PS[2][:, 0, 0:256], HD ** -0.5, BIAS[:],
                                           ALU.mult, ALU.add).then_inc(zn_dve, 1)
            for i in range(4):
                dve.wait_ge(vt_done, i + 1)
                nc.vector.tensor_copy(VP[:, i, :], PS[i // 2][:, i % 2, :]).then_inc(vp_ready, 1)
            dve.wait_ge(ev_act, 16)
            step = 0
            for g in range(4):
                d = 1 << g
                src, dst = (UP, UA, UB, UA)[g], (UA, UB, UA, UB)[g]
                lo = 2 * d - 1
                if g:
                    dve.wait_ge(pool_step, step)
                nc.vector.tensor_tensor(dst[:, g:4, lo:528], src[:, g:4, lo:528], src[:, g:4, lo - d:528 - d],
                                        ALU.add).then_inc(pool_step, 1)
                step += 1
            dve.wait_ge(pool_step, step)
            for g, w in enumerate(WINDOWS):
                r = (UA, UB)[g % 2]
                nc.vector.tensor_tensor(r[:, g, 16:32], r[:, g, 16:32], RCP[:, g, :], ALU.mult)
                nc.vector.scalar_tensor_tensor(r[:, g, 32:528], r[:, g, 32:528], 1.0 / w, UP[:, g, 32:528],
                                               ALU.mult, ALU.subtract)
                last = nc.vector.tensor_reduce(UD[:, g, :], US[:, g, :, 16 - w:16], AX.X, ALU.add)
            last.then_inc(pool_step, 1)
            step += 1
            dve.wait_ge(pool_step, step)
            for g, w in enumerate(WINDOWS):
                r = (UA, UB)[g % 2]
                nc.vector.tensor_tensor(r[:, g, 16:32], r[:, g, 16:32], UP[:, g, 16:32], ALU.subtract)
                last = nc.vector.scalar_tensor_tensor(UD[:, g, :], UD[:, g, :], 1.0 / w, US[:, g, :, BUF],
                                                      ALU.mult, ALU.subtract)
            last.then_inc(d_ready, 1)
            dve.wait_ge(zn_act, 3)
            nc.vector.scalar_tensor_tensor(ZN[:, 1, :], ZN[:, 0, :], 0.0, ZN[:, 1, :], ALU.max,
                                           ALU.add).then_inc(zn_dve, 1)
            dve.wait_ge(zn_sum, 1)
            nc.vector.tensor_tensor(ZN[:, 0, :], ZN[:, 0, :], PS[3][:, 0, 64:320], ALU.subtract).then_inc(zn_dve, 1)

            def split_ol(m, seq, dst, cols):
                dve.wait_ge(oh_ready, seq + 1)
                nc.vector.tensor_tensor(OL[:, dst, :, 0:cols], OF[:, m % 2, :, 0:cols],
                                        OH[:, dst, :, 0:cols].bitcast(F32), ALU.subtract).then_inc(ol_ready, 1)

            for g in range(4):
                split_ol(g, g, 4 + g, HT)

            def softplus(h):
                for j in range(4):
                    dve.wait_ge(z_done, 4 * h + j + 1)
                    nc.vector.tensor_scalar(ZS[:, h % 2, OFF[j]:OFF[j] + LEN[j]], PS[0][:, j % 2, 0:LEN[j]],
                                            HD ** -0.5, BIAS[:, h:h + 1], ALU.mult, ALU.add).then_inc(z_dve, 1)
                dve.wait_ge(l_done, h + 1)
                dve.wait_ge(z_dve, 4 * h + 4)
                nc.vector.scalar_tensor_tensor(SP[:, h % 2, :], ZS[:, h % 2, :], 0.0, SP[:, h % 2, :], ALU.max,
                                               ALU.add).then_inc(sp_done, 1)

            softplus(0)
            for h in range(HEADS):
                if h + 1 < HEADS:
                    if h >= 1:
                        dve.wait_ge(w_done, h)
                    softplus(h + 1)
                for i in range(4):
                    dve.wait_ge(s_done, 4 * h + i + 1)
                    z = ZS[:, h % 2, OFF[i]:OFF[i] + LEN[i]]
                    nc.vector.tensor_tensor(z, z, PS[1][:, i % 2, 0:LEN[i]], ALU.subtract).then_inc(lw_done, 1)
                if h % 2:
                    split_ol(h // 2, 4 + h // 2, h // 2, HP)
            dve.wait_ge(kv_used, 2 * NS)
            for r in range(2):
                src = PS[3][r * HD:(r + 1) * HD, 1, 64:128].rearrange("p (b t r) -> p t b r", b=NS, r=2)
                last = nc.vector.tensor_copy(OS[r * HD:(r + 1) * HD], src[:, :, :, r])
            last.then_inc(os_ready, 1)
            dve.wait_ge(oh_ready, 9)
            nc.vector.tensor_tensor(OL[:, 0:4, :, HP:HT], OS[:].rearrange("p t (a b) -> p t a b", a=2),
                                    OH[:, 0:4, :, HP:HT].bitcast(F32), ALU.subtract).then_inc(ol_ready, 1)
            clear_acc(1)
            u0 = BASE["evout"]
            for n in range(8):
                u = u0 + n + 2
                split_lo(u - u % 2, u % 2, width(u))
                add_y(n, n % 2, 1)

        def even_pool(pool):
            def mask(h, ready, done):
                pool.wait_ge(ready, h + 1)
                for j in range(4):
                    m = SP[:, h % 2, OFF[j]:OFF[j] + P]
                    last = nc.gpsimd.affine_select(out=m, in_=m, pattern=[[1, P]], compare_op=ALU.is_gt, fill=0.0,
                                                   base=0, channel_multiplier=-1)
                last.then_inc(done, 1)

            page = {}

            def pages(n):
                src = k_pages if n < NS else v_pages
                if n >= 2:
                    pool.wait_ge(kv_used, n - 1)
                for p in range(PAGES):
                    at_ = n % NS * PAGES + p
                    row = pool.value_load(PT[0:1, at_:at_ + 1], min_val=0, max_val=PHYS - 1)
                    pool.dma_start(KV[:, n % 2, p, :], src[bass.ds(row, 1)].rearrange(
                        "o p n -> (o p) n")).then_inc(kv_in[n % 2], 16)

            pool.wait_ge(h_ready, KC + 1)
            nc.gpsimd.memset(TRI[:], 1.0).then_inc(ident_ok, 1)
            pool.wait_ge(ident_ok, 2)
            nc.gpsimd.affine_select(out=TRI[:], in_=TRI[:], pattern=[[-1, P]], compare_op=ALU.is_ge, fill=0.0,
                                    base=0, channel_multiplier=1).then_inc(ident_ok, 1)
            pool.wait_ge(ev_in, 96)
            for n in range(NS + 2):
                pages(n)
            pool.wait_ge(ev_act, 16)
            pool.wait_ge(ev_dve, 16)
            for dst, src in ((k_t[:, 0:4 * SEQ], KP[:]), (k_t[:, 4 * SEQ:4 * SEQ + 32], QKVS[:, 4:8, :]),
                             (v_t[:, 4 * SEQ:4 * SEQ + 32], QKVS[:, 8:12, :]),
                             (pool_p, UP[:, :, SEQ + 1:SEQ + 16]), (pool_n, US[:, :, :, 1:16])):
                pool.dma_start(dst, src).then_inc(out_done, 16)
            pool.wait_ge(vp_ready, 4)
            pool.dma_start(v_t[:, 0:4 * SEQ], VP[:]).then_inc(out_done, 16)
            mask(0, sp_done, sp_ok)
            for h in range(HEADS):
                if h + 1 < HEADS:
                    mask(h + 1, sp_done, sp_ok)
                mask(h, w_done, w_ok)
                if h + 2 < HEADS:
                    pages(NS + h + 2)

        od_in = sem("od_in"); dec_in = sem("dec_in")
        rot = sem("rot"); turn_half = sem("turn_half"); vg_evac = sem("vg_evac")
        kt_done = sem("kt_done"); kt_evac = sem("kt_evac"); vsf_ready = sem("vsf_ready"); prd_ready = sem("prd_ready")
        vs_done = sem("vs_done"); vs_ready = sem("vs_ready"); vr_done = sem("vr_done"); vr_evac = sem("vr_evac")
        st_in = [sem(f"st_in{i}") for i in range(4)]
        st_out = [sem(f"st_out{i}") for i in range(4)]
        cross_done = sem("cross_done"); vb_done = sem("vb_done"); st_decay = sem("st_decay"); st_new = sem("st_new")
        sc_done = sem("sc_done"); sc_ready = sem("sc_ready"); ret_o = sem("ret_o"); oo_act = sem("oo_act")
        rp_done = sem("rp_done"); rp_evac = sem("rp_evac"); rp_out = sem("rp_out")
        oo_dve = sem("oo_dve"); mean_done = sem("mean_done"); oo_cent = sem("oo_cent"); osq = sem("osq")
        osq_used = sem("osq_used"); oo_norm = sem("oo_norm"); o32_ready = sem("o32_ready")
        ogh_ready = sem("ogh_ready"); ogl_ready = sem("ogl_ready"); xs_step = sem("xs_step"); sel_ok = sem("sel_ok")
        OD = BASE["odin"]

        def head_unit(h, i):
            return OD + 12 * h + i

        def odd_sp(sp, load_unit, load_norm_chunks):
            for h in range(RH):
                for i in range(12):
                    load_unit("odin", 12 * h + i - i % 2, i % 2)
                    if i == 1 and h == 0:
                        load_norm_chunks(4)
                        sp.wait_ge(h_ready, 4 * KC + 1)
                        for dst, src in ((COS[:], rope_c), (SIN[:], rope_s), (KDEC[:], gammas)):
                            sp.dma_start(dst, src).then_inc(od_in, 16)
                    if i == 2:
                        if h:
                            sp.wait_ge(sc_ready, 4 * h)
                        sp.dma_start(DEC[:], decay[h]).then_inc(dec_in, 16)
            for i in range(16):
                load_unit("odout", i - i % 2, i % 2)

        def odd_pe(pe, products, chunk):
            for h in range(RH):
                for i in range(12):
                    u = head_unit(h, i)
                    pe.wait_ge(lo_done, u + 3)
                    if i in (2, 4):
                        pe.wait_ge(turn_half, 2 * h + i // 2)
                    elif i in (3, 5):
                        pe.wait_ge(rot, 2 * h + i // 2)
                    elif i > 5:
                        pe.wait_ge(vg_evac, 8 * h + i - 5)
                    if h and i < 2:
                        pe.wait_ge(oo_act, 4 * h)
                    products(i % 2, i % 2, HH, HL, 0, KC, True, True, (h_ready, 4 * KC) if h + i == 0 else None)
                    c = 6 * h + i // 2
                    if i % 2 and c < ADA_N["odin"]:
                        chunk(ADA_IN["odin"] + c - c % 2, c % 2, 0)
                    if 4 <= i < 8:
                        t = i - 4
                        pe.wait_ge(rot, 2 * h + 2)
                        if t:
                            pe.wait_ge(kt_evac, 4 * h + t)
                        for d in range(2):
                            last = nc.tensor.transpose(PS[2][:, 0, d * P:(d + 1) * P],
                                                       KR[:, d, t * P:(t + 1) * P], IDENT[:])
                        last.then_inc(kt_done, 1)
                    if i == 8:
                        pe.wait_ge(prd_ready, h + 1)
                        nc.tensor.matmul(PS[3][:, 1, 128:144], ONES[:], PRD[:].rearrange("p a b -> p (a b)"),
                                         start=True, stop=True)
                        pe.wait_ge(vsf_ready, h + 1)
                        pe.wait_ge(kt_evac, 4 * h + 4)
                        for t in range(4):
                            last = nc.tensor.transpose(PS[2][0:NS, 0, t * P:(t + 1) * P], VSF[:, t, :], IDENT[:])
                        last.then_inc(vs_done, 1)
                        pe.wait_ge(vs_ready, h + 1)
                    if i >= 8:
                        t = i - 8
                        pe.wait_ge(vr_evac, 4 * h + t) if 4 * h + t else None
                        for f in range(4):
                            last = nc.tensor.transpose(PS[2][:, 0, f * P:(f + 1) * P],
                                                       VFO[:, f, t // 2, (t % 2) * P:(t % 2 + 1) * P], IDENT[:])
                        last.then_inc(vr_done, 1)
                        for k in range(4):
                            n = 16 * h + 4 * t + k
                            b, d = n % 16 // 2, n % 2
                            if d == 0:
                                if n:
                                    pe.wait_ge(st_new, n)
                                nc.tensor.matmul(PS[2][:, 1, :], SEL[0:NS, b, :], VS[0:NS, :],
                                                 start=True, stop=True).then_inc(vb_done, 1)
                            pe.wait_ge(st_in[n % 4], 16 * (n // 4 + 1))
                            for e in range(4):
                                c = 64 + d * 32 + e * 8 + b
                                last = nc.tensor.matmul(PS[3][:, 1, c:c + 1], STATE[n % 4][:, e * P:(e + 1) * P],
                                                        QRS[:, d, b:b + 1], start=True, stop=True)
                            last.then_inc(cross_done, 1)
                pe.wait_ge(vg_evac, 8 * h + 8)
                for j in range(4):
                    for d in range(2):
                        last = nc.tensor.matmul(PS[j // 2][:, j % 2, 0:LEN[j]], KR[:, d, j * P:(j + 1) * P],
                                                QR[:, d, j * P:SEQ], start=(d == 0), stop=(d == 1))
                    last.then_inc(sc_done, 1)
                pe.wait_ge(sc_ready, 4 * h + 4)
                pe.wait_ge(vr_evac, 4 * h + 4)
                for e in range(4):
                    for j in range(4):
                        last = nc.tensor.matmul(PS[e // 2][:, e % 2, j * P:SEQ], VR[:, j, e * P:(e + 1) * P],
                                                SC[:, OFF[j]:OFF[j] + LEN[j]], start=(j == 0), stop=(j == 3))
                    last.then_inc(ret_o, 1)
                pe.wait_ge(st_new, 16 * h + 16)
                for d in range(2):
                    for j in range(4):
                        last = nc.tensor.matmul(PS[2][:, d, :], KT[:, j, d * P:(d + 1) * P], VR[:, j, :],
                                                start=(j == 0), stop=(j == 3))
                    last.then_inc(rp_done, 1)
                pe.wait_ge(rp_evac, 2 * h + 2)
                pe.wait_ge(oo_act, 4 * h + 4)
                pe.wait_ge(oo_dve, h + 1)
                for e in range(4):
                    for half in range(2):
                        last = nc.tensor.matmul(PS[2][:, half, 0:HT], ONES[:], OO[:, e, half, :],
                                                start=(e == 0), stop=(e == 3))
                last.then_inc(mean_done, 1)
                pe.wait_ge(oo_cent, 4 * h + 4)
                for e in range(4):
                    pe.wait_ge(osq, 4 * h + e + 1)
                    for half in range(2):
                        last = nc.tensor.matmul(PS[2][:, half, 0:HT], ONES[:], TR[:, e % 2, half, :],
                                                start=(e == 0), stop=(e == 3))
                    last.then_inc(osq_used, 1)
            u0 = BASE["odout"]
            for n in range(8):
                for half in range(2):
                    pe.wait_ge(lo_done, u0 + 2 * n + half + 3)
                    if half == 0:
                        pe.wait_ge(y_act, 4 * KC + n + 1)
                        pe.wait_ge(y_dve, 4 * KC + n + 1)
                    products(half, n % 2, OGH, OGL, 8 * half, 8, half == 0, half == 1,
                             (ogl_ready, 8 * half) if n == 0 else None)

        def odd_act(act, split_hi, evac_y, rsqrt, counts, load_chunk):
            for h in range(RH):
                gamma = 1.0 - 2.0 ** (-5 - h)
                for i in range(12):
                    u = head_unit(h, i) + 2
                    split_hi(u - u % 2, u % 2, width(u))
                    c = 6 * h + i // 2 + 1
                    if i % 2 and c < ADA_N["odin"]:
                        act.wait_ge(unit_done, u - 1)
                        load_chunk(ADA_IN["odin"] + c - c % 2, c % 2)
                    if i >= 4:
                        act.wait_ge(unit_done, u - 1)
                        if i < 8:
                            nc.scalar.activation(VFO[:, i - 4], PS[i % 2][:, :, 0:HT], ACT.Copy).then_inc(vg_evac, 1)
                        else:
                            nc.scalar.activation(SGO[:, i - 8], PS[i % 2][:, :, 0:HT], ACT.Silu).then_inc(vg_evac, 1)
                            for k in range(4):
                                n = 16 * h + 4 * (i - 8) + k
                                act.wait_ge(cross_done, n + 1)
                                nc.scalar.activation(STATE[n % 4], STATE[n % 4], ACT.Copy,
                                                     scale=gamma).then_inc(st_decay, 1)
                for e in range(4):
                    act.wait_ge(ret_o, 4 * h + e + 1)
                    nc.scalar.activation(OO[:, e, :, 0:HP], halves(PS[e // 2][:, e % 2, 0:SEQ]),
                                         ACT.Copy).then_inc(oo_act, 1)
                for d in range(2):
                    act.wait_ge(rp_done, 2 * h + d + 1)
                    nc.scalar.activation(RP[:, d, :], PS[2][:, d, :], ACT.Copy).then_inc(rp_evac, 1)
                for e in range(4):
                    act.wait_ge(oo_cent, 4 * h + e + 1)
                    if e >= 2:
                        act.wait_ge(osq_used, 4 * h + e - 1)
                    nc.scalar.activation(TR[:, e % 2], OO[:, e], ACT.Square).then_inc(osq, 1)
                rsqrt(counts["r"]); counts["r"] += 1
            for c in range(16):
                act.wait_ge(o32_ready, 16)
                act.wait_ge(rp_out, 32 * RH)
                nc.scalar.activation(OGH[:, c], O32[:, c], ACT.Copy).then_inc(ogh_ready, 1)
            u0 = BASE["odout"]
            for n in range(8):
                for half in range(2):
                    u = u0 + 2 * n + half + 2
                    split_hi(u - u % 2, u % 2, width(u))
                evac_y(n, n % 2, 4, u0 + 2 * n + 1)

        def odd_dve(dve, split_lo, evac_chunk, clear_acc, add_y, refine, counts):
            def turn(k, h, i):
                scale = (1.0, (2 * P) ** -0.5)[k]
                out, outs = ((QR, QRS), (KR, KRS))[k]
                ps = PS[i % 2][:, :, 0:HT]
                base = 6 * (2 * h + k)
                if i % 2 == 0:
                    if 2 * h + k:
                        dve.wait_ge(rot, 2 * h + k)
                    nc.vector.scalar_tensor_tensor(TR[:, 0], ps, scale, COS[:], ALU.mult, ALU.mult)
                    nc.vector.scalar_tensor_tensor(TR[:, 1], ps, scale, SIN[:], ALU.mult,
                                                   ALU.mult).then_inc(turn_half, 1)
                    return
                for part, tab, op in ((0, SIN, ALU.subtract), (1, COS, ALU.add)):
                    m = nc.vector.scalar_tensor_tensor(TR[:, 2], ps, scale, tab[:], ALU.mult, ALU.mult)
                    m.then_inc(rot_step, 1)
                    n_t[0] += 1
                    dve.wait_ge(rot_step, n_t[0])
                    nc.vector.tensor_tensor(halves(out[:, part, :]), TR[:, part, :, 0:HP], TR[:, 2, :, 0:HP], op)
                    last = nc.vector.tensor_tensor(halves(outs[:, part, :]), TR[:, part, :, HP:HT],
                                                   TR[:, 2, :, HP:HT], op)
                    if part == 0:
                        last.then_inc(rot_step, 1)
                        n_t[0] += 1
                        dve.wait_ge(rot_step, n_t[0])
                last.then_inc(rot, 1)

            n_t = [0]
            for h in range(RH):
                gamma = 1.0 - 2.0 ** (-5 - h)
                for i in range(12):
                    u = head_unit(h, i) + 2
                    split_lo(u - u % 2, u % 2, width(u))
                    if i < 4:
                        if h + i == 0:
                            dve.wait_ge(od_in, 48)
                            dve.memset(SEL[0:NS], 0.0).then_inc(sel_ok, 1)
                            dve.wait_ge(sel_ok, 1)
                            for b in range(NS):
                                last = nc.vector.tensor_scalar(SEL[0:NS, b, :], ONES[0:NS, :], IDENT[0:NS, b:b + 1],
                                                               None, ALU.mult)
                            last.then_inc(sel_ok, 1)
                        dve.wait_ge(unit_done, u - 1)
                        turn(i // 2, h, i)
                        if i == 3:
                            dve.wait_ge(rot, 2 * h + 2)
                            nc.vector.tensor_tensor(PRD[:], QRS[:], KRS[:], ALU.mult).then_inc(prd_ready, 1)
                    c = 6 * h + i // 2
                    if i % 2 and c < ADA_N["odin"]:
                        evac_chunk(ADA_IN["odin"] + c - c % 2, c % 2, 0)
                    if 4 <= i < 8:
                        t = i - 4
                        dve.wait_ge(kt_done, 4 * h + t + 1)
                        nc.vector.tensor_scalar(KT[:, t, :], PS[2][:, 0, 0:2 * P], KDEC[:, h, t:t + 1], None,
                                                ALU.mult).then_inc(kt_evac, 1)
                    if i == 8:
                        dve.wait_ge(vg_evac, 8 * h + 4)
                        nc.vector.tensor_copy(VSF[:].rearrange("p t (a b) -> p t a b", a=2),
                                              VFO[:, :, :, HP:HT]).then_inc(vsf_ready, 1)
                        dve.wait_ge(vs_done, h + 1)
                        nc.vector.tensor_copy(VS[0:NS, :], PS[2][0:NS, 0, :]).then_inc(vs_ready, 1)
                    if i >= 8:
                        t = i - 8
                        dve.wait_ge(vr_done, 4 * h + t + 1)
                        nc.vector.tensor_copy(VR[:, t, :], PS[2][:, 0, :]).then_inc(vr_evac, 1)
                        for k in range(4):
                            n = 16 * h + 4 * t + k
                            b, d = n % 16 // 2, n % 2
                            dve.wait_ge(st_decay, n + 1)
                            dve.wait_ge(vb_done, n // 2 + 1)
                            nc.vector.scalar_tensor_tensor(STATE[n % 4], PS[2][:, 1, :], KRS[:, d, b:b + 1],
                                                           STATE[n % 4], ALU.mult, ALU.add).then_inc(st_new, 1)
                dve.wait_ge(dec_in, 16 * (h + 1))
                if h:
                    dve.wait_ge(rp_out, 32 * h)
                for j in range(4):
                    dve.wait_ge(sc_done, 4 * h + j + 1)
                    nc.vector.tensor_tensor(SC[:, OFF[j]:OFF[j] + LEN[j]], PS[j // 2][:, j % 2, 0:LEN[j]],
                                            DEC[:, 0:LEN[j]], ALU.mult).then_inc(sc_ready, 1)
                dve.wait_ge(cross_done, 16 * h + 16)
                x = 4 * h
                nc.vector.tensor_copy(XS[:].rearrange("p a t b -> p (a t b)"), PS[3][:, 1, 64:128])
                nc.vector.tensor_copy(QKS[:, 0:2, :].rearrange("p a b -> p (a b)"),
                                      PS[3][:, 1, 128:144]).then_inc(xs_step, 1)
                dve.wait_ge(xs_step, x + 1)
                nc.vector.tensor_tensor(XS[:, 0], XS[:, 0], XS[:, 1], ALU.add)
                nc.vector.tensor_tensor(QKS[:, 2, :], QKS[:, 0, :], QKS[:, 1, :], ALU.add).then_inc(xs_step, 1)
                dve.wait_ge(xs_step, x + 2)
                for e in range(4):
                    last = nc.vector.tensor_tensor(VQ[:, e, :], VSF[:, e, :], QKS[:, 2, :], ALU.mult)
                last.then_inc(xs_step, 1)
                dve.wait_ge(xs_step, x + 3)
                nc.vector.scalar_tensor_tensor(XS[:, 0], XS[:, 0], gamma, VQ[:], ALU.mult, ALU.add).then_inc(xs_step, 1)
                dve.wait_ge(xs_step, x + 4)
                nc.vector.tensor_copy(OO[:, :, :, HP:HT],
                                      XS[:, 0].rearrange("p t (a b) -> p t a b", a=2)).then_inc(oo_dve, 1)
                dve.wait_ge(mean_done, h + 1)
                for e in range(4):
                    nc.vector.scalar_tensor_tensor(OO[:, e], PS[2][:, :, 0:HT], -1.0 / RV, OO[:, e], ALU.mult,
                                                   ALU.add).then_inc(oo_cent, 1)
                r = counts["r"]; counts["r"] += 1
                dve.wait_ge(osq_used, 4 * h + 4)
                nc.vector.tensor_scalar(VAR[:], PS[2][:, :, 0:HT], 1.0 / RV, 1e-5, ALU.mult, ALU.add).then_inc(var_ok, 1)
                refine(r)
                for e in range(4):
                    nc.vector.tensor_tensor(OO[:, e], OO[:, e], RS[:], ALU.mult).then_inc(oo_norm, 1)
                dve.wait_ge(oo_norm, 4 * h + 4)
                for e in range(4):
                    nc.vector.tensor_tensor(O32[:, 4 * h + e], OO[:, e], SGO[:, e], ALU.mult).then_inc(o32_ready, 1)
            for c in range(16):
                dve.wait_ge(ogh_ready, c + 1)
                nc.vector.tensor_tensor(OGL[:, c], O32[:, c], OGH[:, c].bitcast(F32),
                                        ALU.subtract).then_inc(ogl_ready, 1)
            clear_acc(4)
            u0 = BASE["odout"]
            for n in range(8):
                for half in range(2):
                    u = u0 + 2 * n + half + 2
                    split_lo(u - u % 2, u % 2, width(u))
                add_y(n, n % 2, 4)

        rot_step = sem("rot_step")

        def odd_pool(pool):
            def state_in(n):
                pool.dma_start(STATE[n % 4], ret_past[n]).then_inc(st_in[n % 4], 16)

            pool.wait_ge(h_ready, 4 * KC + 1)
            for n in range(4):
                state_in(n)
            for h in range(RH):
                for n in range(16 * h, 16 * h + 16):
                    pool.wait_ge(st_new, n + 1)
                    pool.dma_start(ret_n[n], STATE[n % 4]).then_inc(st_out[n % 4], 16)
                    if n >= 1 and n + 3 < 16 * RH:
                        pool.wait_ge(st_out[(n - 1) % 4], 16 * ((n - 1) // 4 + 1))
                        state_in(n + 3)
                for d in range(2):
                    pool.wait_ge(rp_evac, 2 * h + d + 1)
                    pool.dma_start(ret_p[h, d], RP[:, d, :]).then_inc(rp_out, 16)

        block = ctx.enter_context(nc.Block())
        unit_src = {}
        for name, n, w in PLAN:
            if name[:2] == "in":
                unit_src[name] = (w_in, int(name[2]) * 2 * FC)
            elif name[:3] == "out":
                unit_src[name] = (w_out, int(name[3]) * 16)
            else:
                unit_src[name] = ({"evin": w_even, "evout": w_evout, "odin": w_odd, "odout": w_odout}[name], 0)

        @block.sync
        def _(sp):
            def load_unit(name, i, s):
                src, first = unit_src[name]
                w = WIDTH[BASE[name]]
                row = src[first + i + s]
                u = BASE[name] + i
                sp.wait_ge(lo_done, u + s + 1)
                sp.dma_start(RAW[:, s, 0:w], row).then_inc(raw_in[s], 16)

            def load_norm_chunks(b):
                c0 = 16 + 24 * b
                for c in range(c0, c0 + AT_NORM[b] + (b < 6)):
                    sp.wait_ge(ada_mm, c + 1)
                    sp.dma_start(AW[:, c % 2, :], w_ada[c]).then_inc(ada_in[c % 2], 16)

            def load_ffn(f, b):
                load_unit(f"in{f}", 0, 0)
                load_unit(f"in{f}", 0, 1)
                load_norm_chunks(b)
                with sp.Fori(1, FC) as j:
                    load_unit(f"in{f}", 2 * j, 0)
                    load_unit(f"in{f}", 2 * j, 1)
                with sp.Fori(0, 8) as i:
                    for s in range(2):
                        load_unit(f"out{f}", 2 * i, s)

            sp.dma_start(CS[:], c_t).then_inc(c_in, 16)
            sp.dma_start(SA1[:], b_ada).then_inc(tab_in, 16)
            sp.dma_start(GAIN[:, 0:48], g_pre).then_inc(tab_in, 16)
            sp.dma_start(GAIN[:, 48:96], g_post).then_inc(tab_in, 16)
            sp.dma_start(X[:], x_t).then_inc(x_in, 16)
            for q in range(4):
                sp.dma_start(AFIRST[:, 4 * q:4 * q + 4, :],
                             w_ada[4 * q:4 * q + 4].rearrange("c p n -> p c n")).then_inc(first_in[q], 16)
            load_ffn(0, 0)
            even_sp(sp, load_unit, load_norm_chunks)
            load_ffn(1, 2)
            load_ffn(2, 3)
            odd_sp(sp, load_unit, load_norm_chunks)
            load_ffn(3, 5)
            sp.wait_ge(out_done, 96)
            sp.wait_ge(rp_out, 32 * RH)
            for q in st_out:
                sp.wait_ge(q, 256)
            sp.wait_ge(y_out, 16 * KC)

        @block.tensor
        def _(pe):
            def chunk_products(out, w):
                for k in range(KC):
                    last = nc.tensor.matmul(out, w[:, k * P:(k + 1) * P], CS[:, k, :],
                                            start=(k == 0), stop=(k == KC - 1))
                last.then_inc(ada_mm, 1)

            def chunk(i, s, bank=None):
                pe.wait_ge(ada_in[s], 8 * (i - 16) + 16)
                pe.wait_ge(ada_evac, i + s + 1 if bank is None else i + s + 2)
                chunk_products(ADAP[:, s if bank is None else bank, 0:NB], AW[:, s, :])

            def norm_chunks(b, first, end):
                for k in range(first, min(end, AT_NORM[b])):
                    c = 16 + 24 * b + k
                    pe.wait_ge(ada_in[c % 2], 16 * (c // 2 - 7))
                    if k < 2:
                        pe.wait_ge(ada_evac, 16 + 24 * b + 2)
                    chunk_products(ADAP[:, k % 2, 16 * (k // 2):16 * (k // 2) + NB], AW[:, c % 2, :])

            def products(s, pair, xh, xl, k0, n, first, last_k, per_chunk=None):
                for k in range(n):
                    if per_chunk is not None:
                        pe.wait_ge(per_chunk[0], per_chunk[1] + k + 1)
                    for t, (w, x) in enumerate(((WH, xh), (WH, xl), (WL, xh))):
                        for half in range(2):
                            last = nc.tensor.matmul(
                                PS[pair][:, half, 0:HT], w[:, s, k * P:(k + 1) * P], x[:, k0 + k, half, :],
                                start=(first and k == 0 and t == 0), stop=(last_k and k == n - 1 and t == 2))
                last.then_inc(unit_done, 1)

            def ffn(f):
                u0, o0, c0 = BASE[f"in{f}"], BASE[f"out{f}"], ADA_IN[f"in{f}"]
                sub = SUB[f"out{f}"]

                def body(i, ada, first):
                    for s in range(2):
                        j = 2 * i + s
                        u = u0 + 2 * j
                        wait_h = (h_ready, KC * sub) if first and s == 0 else None
                        pe.wait_ge(lo_done, u + 3)
                        pe.wait_ge(gate_evac, FC * f + j + 1)
                        products(0, 0, HH, HL, 0, KC, True, True, wait_h)
                        pe.wait_ge(lo_done, u + 4)
                        pe.wait_ge(up_evac, FC * f + j + 2)
                        products(1, 1, HH, HL, 0, KC, True, True)
                        if ada:
                            chunk(c0 + 2 * i, s)
                n_ada = ADA_N[f"in{f}"] // 2
                body(0, True, True)
                with pe.Fori(1, n_ada) as i:
                    body(i, True, False)
                with pe.Fori(n_ada, 11) as i:
                    body(i, False, False)
                pe.wait_ge(gl_done, FC * (f + 1))
                with pe.Fori(0, 4) as i:
                    for s in range(2):
                        n = 2 * i + s
                        pe.wait_ge(y_act, KC * sub + n + 1)
                        pe.wait_ge(y_dve, KC * sub + n + 1)
                        for half in range(2):
                            pe.wait_ge(lo_done, o0 + 4 * i + 2 * s + half + 3)
                            products(half, s, GH, GL, 11 * half, 11, half == 0, half == 1)

            def sum_squares(src, start, stop):
                for half in range(2):
                    last = nc.tensor.matmul(ST[:, half, 0:HT], ONES[:], src[:, half, :], start=start, stop=stop)
                return last

            def boundary(b):
                if b > 0:
                    pe.wait_ge(acc_step, 9 * b)
                    sum_squares(ACC[:], True, True).then_inc(sum_done, 1)
                norm_chunks(b, 0, BEFORE_SUMS[b])
                if b < 6:
                    for c in range(KC):
                        pe.wait_ge(sq_ready, KC * b + c + 1)
                        last = sum_squares(SQ[:, c % 2], c == 0, c == KC - 1)
                        last.then_inc(sq_used, 1)
                if b == 0:
                    for c in range(16):
                        pe.wait_ge(first_in[c // 4], 16)
                        pe.wait_ge(ada_evac, c + 1)
                        chunk_products(ADAP[:, c % 2, 0:NB], AFIRST[:, c, :])
                norm_chunks(b, BEFORE_SUMS[b], AT_NORM[b])

            pe.wait_ge(silu_c, 1)
            pe.wait_ge(const_ok, 1)
            boundary(0)
            ffn(0)
            boundary(1)
            even_pe(pe, products, chunk)
            boundary(2)
            ffn(1)
            boundary(3)
            ffn(2)
            boundary(4)
            odd_pe(pe, products, chunk)
            boundary(5)
            ffn(3)
            boundary(6)

        @block.scalar
        def _(act):
            def split_hi(i, s, w):
                if w:
                    act.wait_ge(unit_done, i + s - 1)
                    act.wait_ge(raw_in[s], 8 * i + 16)
                    nc.scalar.activation(WH[:, s, 0:w], RAW[:, s, 0:w], ACT.Copy).then_inc(hi_done, 1)

            def first_units():
                for s in range(2):
                    act.wait_ge(raw_in[s], 16)
                    nc.scalar.activation(WH[:, s, 0:W8], RAW[:, s, 0:W8], ACT.Copy).then_inc(hi_done, 1)

            def evac_y(n, pair, sub, u):
                act.wait_ge(acc_step, 9 * sub + n + 1)
                act.wait_ge(unit_done, u + 1)
                act.wait_ge(const_ok, 1)
                nc.scalar.activation(SQ[:, pair], PS[pair][:, :, 0:HT], ACT.Square)
                nc.scalar.activation(Y[:, n, :, 0:HP], PS[pair][:, :, 0:HP], ACT.Copy,
                                     scale=MOD[:, 24 * sub + 16 + n, 0:1]).then_inc(y_act, 1)

            def load_chunk(i, s):
                act.dma_start(AW[:, s, :], w_ada[i + s]).then_inc(ada_in[s], 16)

            def ffn(f):
                u0, o0 = BASE[f"in{f}"], BASE[f"out{f}"]
                sub = SUB[f"out{f}"]
                c0 = ADA_IN[f"in{f}"]

                def body(i, widths, loads=(False, False)):
                    for s in range(2):
                        j = 2 * i + s
                        u = u0 + 2 * j
                        split_hi(u + 2, 0, widths[2 * s])
                        act.wait_ge(up_evac, FC * f + j + 1)
                        act.wait_ge(unit_done, u + 1)
                        if loads[s]:
                            load_chunk(c0 + 2 * i + 2 * s, 1 - s)
                        nc.scalar.activation(SG[:, s], PS[0][:, :, 0:HT], ACT.Silu).then_inc(gate_evac, 1)
                        split_hi(u + 2, 1, widths[2 * s + 1])
                        act.wait_ge(up_evac, FC * f + j + 3)
                        act.wait_ge(const_ok, 1)
                        nc.scalar.activation(GH[:, j], G32[:, s], ACT.Copy).then_inc(gh_done, 1)
                n_ada = ADA_N[f"in{f}"] // 2
                with act.Fori(0, n_ada - 1) as i:
                    body(i, [W8] * 4, (True, True))
                body(n_ada - 1, [W8] * 4, (True, False))
                with act.Fori(n_ada, 10) as i:
                    body(i, [W8] * 4)
                body(10, [W8, W8, W11, W11])

                def body_out(i, widths):
                    for s in range(2):
                        n = 2 * i + s
                        u = o0 + 2 * n
                        split_hi(u + 2, 0, widths[2 * s])
                        split_hi(u + 2, 1, widths[2 * s + 1])
                        evac_y(n, s, sub, u + 1)
                with act.Fori(0, 3) as i:
                    body_out(i, [W11] * 4)
                nxt = width(o0 + 16)
                body_out(3, [W11, W11, nxt, nxt])

            def rsqrt(r):
                act.wait_ge(var_ok, r + 1)
                nc.scalar.activation(RS[:], VAR[:], ACT.Ln).then_inc(ln_ok, 1)
                act.wait_ge(ln_ok, r + 1)
                nc.scalar.activation(RS[:], RS[:], ACT.Exp, scale=-0.5).then_inc(exp_ok, 1)

            def boundary(b, counts):
                if b > 0:
                    rsqrt(counts["r"]); counts["r"] += 1
                if b < 6:
                    for c in range(KC):
                        if b > 0:
                            act.wait_ge(x_upd, KC * (b - 1) + c + 1)
                        if KC * b + c >= 2:
                            act.wait_ge(sq_used, KC * b + c - 1)
                        if b == 0 and c == 0:
                            act.wait_ge(x_in, 16)
                        nc.scalar.activation(SQ[:, c % 2], X[:, c], ACT.Square).then_inc(sq_ready, 1)
                    rsqrt(counts["r"]); counts["r"] += 1
                    if b == 0:
                        first_units()
                        act.wait_ge(ada_evac, 16 + 2)
                    for c in range(KC):
                        act.wait_ge(t_ready, KC * b + c + 1)
                        nc.scalar.activation(Y[:, c, :, 0:HP], Y[:, c, :, 0:HP], ACT.Identity,
                                             bias=MOD[:, 24 * b + c, 0:1],
                                             scale=MOD[:, 24 * b + 8 + c, 0:1]).then_inc(h32_ready, 1)
                    for c in range(KC):
                        act.wait_ge(samp, 2 * b + 2)
                        act.wait_ge(h32_ready, KC * b + c + 1)
                        nc.scalar.activation(HH[:, c], Y[:, c], ACT.Copy).then_inc(hh_ready, 1)

            counts = {"r": 0}
            act.wait_ge(c_in, 16)
            nc.scalar.activation(CS[:], CS[:], ACT.Silu).then_inc(silu_c, 1)
            boundary(0, counts)
            ffn(0)
            boundary(1, counts)
            even_act(act, split_hi, evac_y, load_chunk)
            boundary(2, counts)
            ffn(1)
            boundary(3, counts)
            ffn(2)
            boundary(4, counts)
            odd_act(act, split_hi, evac_y, rsqrt, counts, load_chunk)
            boundary(5, counts)
            ffn(3)
            boundary(6, counts)

        @block.vector
        def _(dve):
            def split_lo(i, s, w):
                if w:
                    dve.wait_ge(hi_done, i + s + 1)
                    nc.vector.tensor_tensor(WL[:, s, 0:w], RAW[:, s, 0:w], WH[:, s, 0:w].bitcast(F32),
                                            ALU.subtract).then_inc(lo_done, 1)

            def evac_chunk(i, s, bank=None):
                dve.wait_ge(ada_mm, i + s + 3)
                nc.vector.tensor_scalar(MOD[:, i + s, :], ADAP[:, s if bank is None else bank, 0:NB], SA1[:, bass.ds(i + s, 1)],
                                        SA2[:, bass.ds(i + s, 1)], ALU.add, ALU.mult).then_inc(ada_evac, 1)

            def clear_acc(sub):
                if sub:
                    dve.wait_ge(sum_done, sub)
                nc.vector.memset(ACC[:], 0.0).then_inc(acc_step, 1)

            def add_y(n, pair, sub):
                dve.wait_ge(y_act, KC * sub + n + 3)
                nc.vector.tensor_tensor(
                    Y[:, n, :, HP:HT], PS[pair][:, :, HP:HT],
                    MOD[:, 24 * sub + 16 + n, 1:NB].rearrange("p (a b) -> p a b", a=2),
                    ALU.mult).then_inc(y_dve, 1)
                dve.wait_ge(acc_step, 9 * sub + n + 1)
                nc.vector.tensor_tensor(ACC[:], ACC[:], SQ[:, pair], ALU.add).then_inc(acc_step, 1)

            def ffn(f):
                u0, o0, c0 = BASE[f"in{f}"], BASE[f"out{f}"], ADA_IN[f"in{f}"]
                sub = SUB[f"out{f}"]

                def body(i, widths, ada):
                    for s in range(2):
                        j = 2 * i + s
                        u = u0 + 2 * j
                        split_lo(u + 2, 0, widths[2 * s])
                        split_lo(u + 2, 1, widths[2 * s + 1])
                        dve.wait_ge(gate_evac, FC * f + j + 2)
                        dve.wait_ge(unit_done, u + 2)
                        nc.vector.tensor_tensor(G32[:, s], SG[:, s], PS[1][:, :, 0:HT],
                                                ALU.mult).then_inc(up_evac, 1)
                        if ada:
                            evac_chunk(c0 + 2 * i, s)
                        dve.wait_ge(gh_done, FC * f + j + 1)
                        nc.vector.tensor_tensor(GL[:, j], G32[:, s], GH[:, j].bitcast(F32),
                                                ALU.subtract).then_inc(gl_done, 1)
                n_ada = ADA_N[f"in{f}"] // 2
                with dve.Fori(0, n_ada) as i:
                    body(i, [W8] * 4, True)
                with dve.Fori(n_ada, 10) as i:
                    body(i, [W8] * 4, False)
                body(10, [W8, W8, W11, W11], False)
                clear_acc(sub)

                def body_out(i, widths):
                    for s in range(2):
                        n = 2 * i + s
                        u = o0 + 2 * n
                        split_lo(u + 2, 0, widths[2 * s])
                        split_lo(u + 2, 1, widths[2 * s + 1])
                        add_y(n, s, sub)
                with dve.Fori(0, 3) as i:
                    body_out(i, [W11] * 4)
                nxt = width(o0 + 16)
                body_out(3, [W11, W11, nxt, nxt])

            def variance(r, src, scale, eps):
                nc.vector.tensor_scalar(VAR[:], src, scale, eps, ALU.mult, ALU.add).then_inc(var_ok, 1)

            def refine(r):
                dve.wait_ge(exp_ok, r + 1)
                nc.vector.scalar_tensor_tensor(NT[:], RS[:], -0.5, VAR[:], ALU.mult, ALU.mult).then_inc(newton, 1)
                dve.wait_ge(newton, 3 * r + 1)
                nc.vector.tensor_tensor(NT[:], NT[:], RS[:], ALU.mult).then_inc(newton, 1)
                dve.wait_ge(newton, 3 * r + 2)
                nc.vector.scalar_tensor_tensor(RS[:], NT[:], 1.5, RS[:], ALU.add, ALU.mult).then_inc(newton, 1)
                dve.wait_ge(newton, 3 * r + 3)

            def boundary(b, counts):
                if b > 0:
                    r = counts["r"]; counts["r"] += 1
                    dve.wait_ge(sum_done, b)
                    variance(r, ST[:, :, 0:HT], 1.0 / DM, EPS)
                    refine(r)
                    for c in range(KC + 1):
                        if c < KC:
                            nc.vector.tensor_tensor(Y[:, c], Y[:, c], RS[:], ALU.mult).then_inc(y_scaled, 1)
                        if c > 0:
                            dve.wait_ge(y_scaled, KC * (b - 1) + c)
                            nc.vector.tensor_tensor(X[:, c - 1], X[:, c - 1], Y[:, c - 1],
                                                    ALU.add).then_inc(x_upd, 1)
                if b < 6:
                    r = counts["r"]; counts["r"] += 1
                    dve.wait_ge(sq_used, KC * (b + 1))
                    variance(r, ST[:, :, 0:HT], 1.0 / DM, EPS)
                    refine(r)
                    if b == 0:
                        dve.wait_ge(x_in, 16)
                    for c in range(KC):
                        nc.vector.tensor_tensor(Y[:, c], X[:, c], RS[:], ALU.mult).then_inc(t_ready, 1)
                    if b == 0:
                        for c in range(0, 16, 2):
                            for s in range(2):
                                evac_chunk(c, s)
                        for s in range(2):
                            split_lo(0, s, W8)
                        dve.wait_ge(ada_evac, 16 + 2)
                    dve.wait_ge(t_ready, KC * (b + 1))
                    for half in range(2):
                        cols = slice(1 + HS * half, 1 + HS * (half + 1))
                        ys = Y[:, :, half, HP:HT]
                        last = nc.vector.tensor_tensor(ys, ys, MOD[:, 24 * b + 8:24 * b + 16, cols], ALU.mult)
                    last.then_inc(samp, 1)
                    dve.wait_ge(samp, 2 * b + 1)
                    for half in range(2):
                        cols = slice(1 + HS * half, 1 + HS * (half + 1))
                        ys = Y[:, :, half, HP:HT]
                        last = nc.vector.tensor_tensor(ys, ys, MOD[:, 24 * b:24 * b + 8, cols], ALU.add)
                    last.then_inc(samp, 1)
                    dve.wait_ge(samp, 2 * b + 2)
                    for c in range(KC):
                        dve.wait_ge(hh_ready, KC * b + c + 1)
                        nc.vector.tensor_tensor(HL[:, c], Y[:, c], HH[:, c].bitcast(F32),
                                                ALU.subtract).then_inc(h_ready, 1)
                    for k in range(AT_NORM[b]):
                        c = 16 + 24 * b + k
                        if k == 0:
                            dve.wait_ge(ada_mm, c + AT_NORM[b] + 2)
                        nc.vector.tensor_scalar(MOD[:, c, :], ADAP[:, k % 2, 16 * (k // 2):16 * (k // 2) + NB],
                                                SA1[:, c:c + 1], SA2[:, c:c + 1], ALU.add,
                                                ALU.mult).then_inc(ada_evac, 1)

            nc.vector.memset(ONES[:], 1.0).then_inc(const_ok, 1)
            dve.sem_inc(lo_done, 2)
            dve.sem_inc(ada_mm, 2)
            dve.sem_inc(ada_evac, 2)
            dve.sem_inc(gate_evac, 1)
            dve.sem_inc(up_evac, 2)
            dve.sem_inc(y_act, 2)
            dve.sem_inc(y_dve, 2)
            dve.wait_ge(tab_in, 48)
            sa1 = SA1[:].rearrange("p (s t c) -> p s t c", s=6, t=3)
            sa2 = SA2[:].rearrange("p (s t c) -> p s t c", s=6, t=3)
            gp = GAIN[:, 0:48].rearrange("p (s c) -> p s c", s=6)
            gq = GAIN[:, 48:96].rearrange("p (s c) -> p s c", s=6)
            nc.vector.tensor_scalar(sa1[:, :, 1, :], sa1[:, :, 1, :], 1.0, None, ALU.add)
            nc.vector.memset(sa2[:, :, 0, :], 1.0)
            nc.vector.tensor_copy(sa2[:, :, 1, :], gp)
            for s in range(6):
                last = nc.vector.tensor_scalar(sa2[:, s, 2, :], gq[:, s, :], 1.0 if s % 3 == 1 else 0.5, None,
                                               ALU.mult)
            last.then_inc(sa_ok, 1)
            dve.wait_ge(sa_ok, 1)
            counts = {"r": 0}
            boundary(0, counts)
            ffn(0)
            boundary(1, counts)
            even_dve(dve, split_lo, evac_chunk, clear_acc, add_y)
            boundary(2, counts)
            ffn(1)
            boundary(3, counts)
            ffn(2)
            boundary(4, counts)
            odd_dve(dve, split_lo, evac_chunk, clear_acc, add_y, refine, counts)
            boundary(5, counts)
            ffn(3)
            boundary(6, counts)

        @block.gpsimd
        def _(pool):
            nc.gpsimd.memset(IDENT[:], 0.0).then_inc(ident_z, 1)
            pool.wait_ge(ident_z, 1)
            nc.gpsimd.affine_select(out=IDENT[:], in_=IDENT[:], pattern=[[-1, P]], compare_op=ALU.not_equal,
                                    fill=1.0, base=0, channel_multiplier=1).then_inc(ident_ok, 1)
            even_pool(pool)
            odd_pool(pool)
            for c in range(KC):
                pool.wait_ge(x_upd, 5 * KC + c + 1)
                pool.dma_start(y_t[:, c], X[:, c].rearrange("p a b -> p (a b)")).then_inc(y_out, 16)


_F = 4


def kernel(x_prompt, x_sample, c_prompt, c_sample, cache_k, cache_v, state_pool, state_ret, page_table, w_ada,
           b_ada, norm_pre, norm_post, ffn_w_in, ffn_w_out, w_in_even, sb_bias, pool_w, pool_scale, w_out_even,
           w_in_odd, w_out_odd):
    import numpy as np
    import concourse.bacc as bacc
    from concourse.bass_utils import run_bass_kernel_spmd as run

    def np_(a):
        return np.asarray(a)

    def tokens(prompt, sample):
        k = prompt.shape[0] // P
        out = np.concatenate([prompt.reshape(k, P, 2, HP), sample.reshape(k, P, 2, HS)], axis=3)
        return out.transpose(1, 0, 2, 3)

    def units(w, ks, order=None):
        k, n = w.shape
        t = w.reshape(k // (ks * P), ks, P, n // P, P).transpose(3, 0, 2, 1, 4)
        if order is not None:
            t = t[order]
        return t.reshape(-1, P, ks * P)

    gate_up = [j + FC * s for j in range(FC) for s in range(2)]
    w_in_u = np.concatenate([units(np_(ffn_w_in)[f // 2, f % 2], KC, gate_up) for f in range(_F)])
    w_out_u = np.concatenate([units(np_(ffn_w_out)[f // 2, f % 2], 11) for f in range(_F)])
    w_ada_u = np.concatenate([units(np_(w_ada)[l], KC) for l in range(2)])
    heads = [n for h in range(RH) for n in
             [2 * h, 2 * h + 1, 8 + 2 * h, 9 + 2 * h] + [16 + 4 * h + e for e in range(4)] +
             [32 + 4 * h + e for e in range(4)]]
    c = np.concatenate([np_(c_prompt), np_(c_sample)])

    half = P
    inv = np.float32(10000.0) ** (-np.arange(half, dtype=np.float32) / np.float32(half))
    pos = np.arange(SEQ + 1, dtype=np.float32)
    ang = (pos[None, :] * inv[:, None]).astype(np.float32)
    rope = [tokens(f(ang)[:, :SEQ].astype(np.float32), np.repeat(f(ang)[:, SEQ:].astype(np.float32), NS, 1))[:, 0]
            for f in (np.cos, np.sin)]
    lg = np.log(1.0 - np.exp2(-5.0 - np.arange(RH, dtype=np.float64)))
    diff = np.arange(SEQ)[None, :] - np.arange(P)[:, None]
    decay = np.stack([np.where(diff >= 0, np.exp(np.maximum(diff, 0) * g), 0.0) for g in lg]).astype(np.float32)
    kdec = np.exp((SEQ - 1.0 - np.arange(SEQ)).reshape(4, P).T[:, None, :] * lg[None, :, None]).astype(np.float32)
    rcp = np.stack([1.0 / np.minimum(np.arange(16) + 1, w) for w in WINDOWS]).astype(np.float32)
    kp = np_(cache_k)[0].reshape(PHYS, P, 4, P).transpose(0, 3, 2, 1).reshape(PHYS, P, 4 * P)
    arrays = {
        "x_t": tokens(np_(x_prompt)[0].T, np_(x_sample)[:, 0].T),
        "c_t": c.T.reshape(KC, P, NB).transpose(1, 0, 2),
        "k_pages": kp,
        "v_pages": np_(cache_v)[0].reshape(PHYS, P, 4 * P),
        "pool_past": np_(state_pool)[0].transpose(2, 0, 1).reshape(4, P, NS, BUF).transpose(1, 0, 2, 3),
        "ret_past": np_(state_ret)[0].transpose(1, 0, 2, 3).reshape(RH * NS * 2, P, RV),
        "table": np_(page_table).reshape(1, NS * PAGES),
        "w_ada": w_ada_u,
        "b_ada": np_(b_ada).reshape(CHUNKS, P).T,
        "g_pre": np_(norm_pre).reshape(48, P).T,
        "g_post": np_(norm_post).reshape(48, P).T,
        "w_in": w_in_u,
        "w_out": w_out_u,
        "w_even": units(np_(w_in_even)[0], KC),
        "w_evout": units(np_(w_out_even)[0], KC),
        "w_odd": units(np_(w_in_odd)[0], KC, heads),
        "w_odout": units(np_(w_out_odd)[0], 8),
        "bias_b": np.broadcast_to(np.tile(np_(sb_bias)[0], PAGES * NS)[None], (P, 256)),
        "pool_w": np_(pool_w)[0].transpose(1, 0, 2),
        "pool_s": np_(pool_scale)[0].reshape(4, P).T,
        "rope_c": rope[0],
        "rope_s": rope[1],
        "decay": decay,
        "gammas": kdec,
        "pool_r": np.broadcast_to(rcp[None], (P, 4, 16)),
    }
    arrays = {f"in_{n}": np.ascontiguousarray(a) for n, a in arrays.items()}
    outs = {"y_t": (P, KC, 2 * HT), "k_t": (P, 4 * SEQ + 32), "v_t": (P, 4 * SEQ + 32), "pool_p": (P, 4, BUF),
            "pool_n": (P, 4, NS, BUF), "ret_p": (RH, 2, P, RV), "ret_n": (RH * NS * 2, P, RV)}

    nc = bacc.Bacc("TRN2", target_bir_lowering=False, num_devices=1)
    args = [nc.dram_tensor(n, a.shape, mybir.dt.from_np(a.dtype), kind="ExternalInput").ap() for n, a in arrays.items()]
    args += [nc.dram_tensor(f"out_{n}", shape, F32, kind="ExternalOutput").ap() for n, shape in outs.items()]
    decoder_step(nc, *args)
    r = run(nc, [arrays], core_ids=[0]).results[0]
    got = {n: np.asarray(r[f"out_{n}"]) for n in outs}

    y = got["y_t"].reshape(P, KC, 2, HT)
    y_prompt = y[..., :HP].transpose(2, 3, 1, 0).reshape(1, SEQ, DM)
    y_sample = y[..., HP:].transpose(2, 3, 1, 0).reshape(NS, 1, DM)
    k = got["k_t"]
    k_prompt = k[:, :4 * SEQ].reshape(P, 4, SEQ).transpose(2, 1, 0).reshape(1, 1, SEQ, HEADS, HD)
    k_sample = k[:, 4 * SEQ:].reshape(P, 4, NS).transpose(2, 1, 0).reshape(1, NS, 1, HEADS, HD)
    v = got["v_t"]
    v_prompt = v[:, :4 * SEQ].reshape(P, 4, 4 * P).transpose(1, 0, 2).reshape(1, 1, SEQ, HEADS, HD)
    v_sample = v[:, 4 * SEQ:].reshape(P, 4, NS).transpose(2, 1, 0).reshape(1, NS, 1, HEADS, HD)
    pool_prompt = got["pool_p"].transpose(2, 1, 0).reshape(1, 1, BUF, 4 * P)
    pool_sample = got["pool_n"].transpose(2, 3, 1, 0).reshape(1, NS, BUF, 4 * P)
    ret_prompt = got["ret_p"].reshape(1, 1, RH, 2 * P, RV)
    ret_sample = got["ret_n"].reshape(RH, NS, 2 * P, RV).transpose(1, 0, 2, 3)[None]
    return tuple(np.ascontiguousarray(a) for a in (y_prompt, y_sample, k_prompt, v_prompt, pool_prompt, ret_prompt,
                                                   k_sample, v_sample, pool_sample, ret_sample))
```
